# Optimizing a Trainium2 kernel written in Bass

```python
import jax, jax.numpy as jnp
from jax import lax
import numpy as np

D_MODEL = 1024
BATCH = 1
SEQ = 256
DEPTH = 1
DEC_BATCH = 8
DEC_SEQ = 8
PAST_LEN = 2048
PAGE_SIZE = 128

N_MEM = 256
D_A = D_MODEL // 2
CONV_A = 3
D_B = D_MODEL // 2
CONV_B = 31
N_XHEADS = 4
XHEAD_DIM = D_MODEL // 8
D_X = N_XHEADS * XHEAD_DIM
N_BRANCH = 3
D_IN = 3 * D_A + 2 * D_B + D_X + N_BRANCH * D_MODEL
N_EXPERTS = 32
TOP_K = 4
D_FF = D_MODEL
SWIGLU_LIMIT = 7.0
SWIGLU_ALPHA = 1.702
MOE_BLOCK = 128
EPS = 1e-5

kernel_name = 'hybrid_gatedconv_conformer_memxattn_moe_step'

def _rmsnorm(x, g):
    xf = x.astype(jnp.float32)
    y = xf * lax.rsqrt(jnp.mean(xf * xf, axis=-1, keepdims=True) + EPS)
    return (y * g.astype(jnp.float32)).astype(x.dtype)

def _layernorm(x, g, b):
    xf = x.astype(jnp.float32)
    mu = jnp.mean(xf, axis=-1, keepdims=True)
    xc = xf - mu
    var = jnp.mean(xc * xc, axis=-1, keepdims=True)
    return (xc * lax.rsqrt(var + EPS) * g.astype(jnp.float32) + b.astype(jnp.float32)).astype(x.dtype)

def _causal_dwconv(buf, u, w):
    ext = jnp.concatenate([buf.astype(u.dtype), u], axis=1)
    y = lax.conv_general_dilated(ext, w[:, None, :].astype(u.dtype), window_strides=(1,), padding='VALID',
                                 dimension_numbers=('NWC', 'WIO', 'NWC'), feature_group_count=u.shape[-1])
    return y, ext[:, ext.shape[1] - (w.shape[0] - 1):]

def _memory_kv(mem, g, w_kv):
    kv = _rmsnorm(mem, g) @ w_kv
    k, v = jnp.split(kv, 2, axis=-1)
    bm, m, _ = mem.shape
    return k.reshape(bm, m, N_XHEADS, XHEAD_DIM), v.reshape(bm, m, N_XHEADS, XHEAD_DIM)

def _mixer_block(x, buf_a, buf_b, mem_k, mem_v, norm_mix, w_in, w_conv_a, w_out_a, w_conv_b, b_conv_b,
                 ln_g, ln_b, w_out_b, w_out_x, w_o):
    bn, s, _ = x.shape
    h = _rmsnorm(x, norm_mix)
    z = h @ w_in
    cuts = [D_A, 2 * D_A, 3 * D_A, 3 * D_A + D_B, 3 * D_A + 2 * D_B, 3 * D_A + 2 * D_B + D_X]
    a_b, a_c, a_h, b_val, b_gate, q, g = jnp.split(z, cuts, axis=-1)
    conv_a, new_buf_a = _causal_dwconv(buf_a, a_c * a_h, w_conv_a)
    y_a = (a_b * conv_a) @ w_out_a
    conv_b, new_buf_b = _causal_dwconv(buf_b, b_val * jax.nn.sigmoid(b_gate), w_conv_b)
    y_b = jax.nn.silu(_layernorm(conv_b + b_conv_b, ln_g, ln_b)) @ w_out_b
    qh = q.reshape(bn, s, N_XHEADS, XHEAD_DIM)
    sc = jnp.einsum('bshd,bmhd->bhsm', qh, mem_k.astype(qh.dtype), preferred_element_type=jnp.float32) * (XHEAD_DIM ** -0.5)
    p = jax.nn.softmax(sc, axis=-1).astype(mem_v.dtype)
    o = jnp.einsum('bhsm,bmhd->bshd', p, mem_v).reshape(bn, s, D_X)
    y_x = o @ w_out_x
    gates = jax.nn.sigmoid(g.reshape(bn, s, N_BRANCH, D_MODEL))
    merged = gates[:, :, 0] * y_a + gates[:, :, 1] * y_b + gates[:, :, 2] * y_x
    return x + merged @ w_o, new_buf_a, new_buf_b

def _moe(h, w_router, b_router, w_gu, b_gu, w_dn, b_dn):
    t, d = h.shape
    tk = t * TOP_K
    logits = jnp.dot(h, w_router, preferred_element_type=jnp.float32) + b_router.astype(jnp.float32)
    top_v, top_e = lax.top_k(logits, TOP_K)
    gate = jax.nn.softmax(top_v, axis=-1)
    flat_e = top_e.reshape(tk)
    flat_t = jnp.arange(tk, dtype=jnp.int32) // TOP_K
    flat_g = gate.reshape(tk)
    counts = jnp.bincount(flat_e, length=N_EXPERTS)
    padded = (counts + MOE_BLOCK - 1) // MOE_BLOCK * MOE_BLOCK
    pad_end = jnp.cumsum(padded)
    pad_start = pad_end - padded
    start = jnp.cumsum(counts) - counts
    order = jnp.argsort(flat_e)
    e_sorted = flat_e[order]
    dest = pad_start[e_sorted] + jnp.arange(tk, dtype=jnp.int32) - start[e_sorted]
    n_blocks = -(-tk // MOE_BLOCK) + N_EXPERTS
    n_slots = n_blocks * MOE_BLOCK
    slot_tok = jnp.full((n_slots,), t, jnp.int32).at[dest].set(flat_t[order])
    slot_w = jnp.zeros((n_slots,), jnp.float32).at[dest].set(flat_g[order])
    block_e = jnp.minimum(jnp.searchsorted(pad_end, jnp.arange(n_blocks, dtype=jnp.int32) * MOE_BLOCK, side='right'),
                          N_EXPERTS - 1)
    h_pad = jnp.concatenate([h, jnp.zeros((1, d), h.dtype)], axis=0)
    xb = h_pad[slot_tok].reshape(n_blocks, MOE_BLOCK, d)

    def expert_block(args):
        xe, e = args
        gu = xe @ w_gu[e] + b_gu[e]
        gt, up = jnp.split(gu, 2, axis=-1)
        gt = jnp.minimum(gt, SWIGLU_LIMIT)
        up = jnp.clip(up, -SWIGLU_LIMIT, SWIGLU_LIMIT)
        act = gt * jax.nn.sigmoid(SWIGLU_ALPHA * gt) * (up + 1.0)
        return act @ w_dn[e] + b_dn[e]

    out = lax.map(expert_block, (xb, block_e)).reshape(n_slots, d)
    y = jax.ops.segment_sum(out * slot_w[:, None].astype(out.dtype), slot_tok, num_segments=t + 1)
    return y[:t]

def _ffn_block(x, norm_ffn, w_router, b_router, w_gu, b_gu, w_dn, b_dn):
    bn, s, d = x.shape
    h = _rmsnorm(x, norm_ffn).reshape(bn * s, d)
    return x + _moe(h, w_router, b_router, w_gu, b_gu, w_dn, b_dn).reshape(bn, s, d)

def setup_inputs(seed: int = 0) -> dict:
    key = jax.random.key(seed)
    ks = jax.random.split(key, 40)
    D = D_MODEL
    L = DEPTH

    def nrm(k, shape, scale):
        return scale * jax.random.normal(k, shape, jnp.float32)

    return {
        'x_prompt': nrm(ks[0], (BATCH, SEQ, D), 1.0),
        'x_sample': nrm(ks[1], (DEC_BATCH, DEC_SEQ, D), 1.0),
        'mem_prompt': nrm(ks[2], (BATCH, N_MEM, D), 1.0),
        'state_conv_a': nrm(ks[3], (L, DEC_BATCH, CONV_A - 1, D_A), 1.0),
        'state_conv_b': nrm(ks[4], (L, DEC_BATCH, CONV_B - 1, D_B), 0.5),
        'cache_mem_k': nrm(ks[5], (L, DEC_BATCH, N_MEM, N_XHEADS, XHEAD_DIM), 1.0),
        'cache_mem_v': nrm(ks[6], (L, DEC_BATCH, N_MEM, N_XHEADS, XHEAD_DIM), 1.0),
        'norm_mix': 1.0 + nrm(ks[7], (L, D), 0.02),
        'w_in': nrm(ks[8], (L, D, D_IN), D ** -0.5),
        'w_conv_a': nrm(ks[9], (L, CONV_A, D_A), CONV_A ** -0.5),
        'w_out_a': nrm(ks[10], (L, D_A, D), D_A ** -0.5),
        'w_conv_b': nrm(ks[11], (L, CONV_B, D_B), CONV_B ** -0.5),
        'b_conv_b': nrm(ks[12], (L, D_B), 0.02),
        'ln_conv_b_g': 1.0 + nrm(ks[13], (L, D_B), 0.02),
        'ln_conv_b_b': nrm(ks[14], (L, D_B), 0.02),
        'w_out_b': nrm(ks[15], (L, D_B, D), D_B ** -0.5),
        'norm_mem': 1.0 + nrm(ks[16], (L, D), 0.02),
        'w_mem_kv': nrm(ks[17], (L, D, 2 * D_X), D ** -0.5),
        'w_out_x': nrm(ks[18], (L, D_X, D), D_X ** -0.5),
        'w_o': nrm(ks[19], (L, D, D), D ** -0.5),
        'norm_ffn': 1.0 + nrm(ks[20], (L, D), 0.02),
        'w_router': nrm(ks[21], (L, D, N_EXPERTS), D ** -0.5),
        'b_router': nrm(ks[22], (L, N_EXPERTS), 0.01),
        'w_gu': nrm(ks[23], (L, N_EXPERTS, D, 2 * D_FF), D ** -0.5),
        'b_gu': nrm(ks[24], (L, N_EXPERTS, 2 * D_FF), 0.01),
        'w_dn': nrm(ks[25], (L, N_EXPERTS, D_FF, D), D_FF ** -0.5),
        'b_dn': nrm(ks[26], (L, N_EXPERTS, D), 0.01),
        'norm_final': 1.0 + nrm(ks[27], (D,), 0.02),
    }

def reference(x_prompt, x_sample, mem_prompt, state_conv_a, state_conv_b, cache_mem_k, cache_mem_v,
              norm_mix, w_in, w_conv_a, w_out_a, w_conv_b, b_conv_b, ln_conv_b_g, ln_conv_b_b, w_out_b,
              norm_mem, w_mem_kv, w_out_x, w_o, norm_ffn, w_router, b_router, w_gu, b_gu, w_dn, b_dn,
              norm_final):
    yp, ys = x_prompt, x_sample
    bp = x_prompt.shape[0]
    pa, pb, pk, pv, sa, sb = [], [], [], [], [], []
    for l in range(DEPTH):
        mix_w = (norm_mix[l], w_in[l], w_conv_a[l], w_out_a[l], w_conv_b[l], b_conv_b[l],
                 ln_conv_b_g[l], ln_conv_b_b[l], w_out_b[l], w_out_x[l], w_o[l])
        ffn_w = (norm_ffn[l], w_router[l], b_router[l], w_gu[l], b_gu[l], w_dn[l], b_dn[l])
        k_p, v_p = _memory_kv(mem_prompt, norm_mem[l], w_mem_kv[l])
        zero_a = jnp.zeros((bp, CONV_A - 1, D_A), x_prompt.dtype)
        zero_b = jnp.zeros((bp, CONV_B - 1, D_B), x_prompt.dtype)
        yp, na_p, nb_p = _mixer_block(yp, zero_a, zero_b, k_p, v_p, *mix_w)
        yp = _ffn_block(yp, *ffn_w)
        ys, na_s, nb_s = _mixer_block(ys, state_conv_a[l], state_conv_b[l], cache_mem_k[l], cache_mem_v[l], *mix_w)
        ys = _ffn_block(ys, *ffn_w)
        pa.append(na_p)
        pb.append(nb_p)
        pk.append(k_p)
        pv.append(v_p)
        sa.append(na_s)
        sb.append(nb_s)
    y_prompt = _rmsnorm(yp, norm_final)
    y_sample = _rmsnorm(ys, norm_final)
    return (y_prompt, y_sample, jnp.stack(pa), jnp.stack(pb), jnp.stack(pk), jnp.stack(pv), jnp.stack(sa), jnp.stack(sb))


_drawn_inputs = setup_inputs


def setup_inputs(seed=0):
    import zlib

    import numpy as np

    out = dict(_drawn_inputs(seed))
    spreads = {}
    factors = {'ln_conv_b_b': 2.735,
     'norm_mem': 2.854,
     'b_router': 3.011,
     'b_gu': 8.0,
     'b_dn': 8.0,
     'norm_final': 9.64,
     'ln_conv_b_g': 2.717}
    for name, (base, spread) in spreads.items():
        noise = np.random.default_rng([zlib.crc32(name.encode()), seed]).standard_normal(out[name].shape)
        drawn = base * np.exp(spread * noise) if base else spread * noise
        out[name] = __import__('jax').numpy.asarray(drawn.astype(out[name].dtype))
    for name, factor in factors.items():
        out[name] = (out[name] * factor).astype(out[name].dtype)
    return out
```

```python
import concourse.bass as bass
from concourse import mybir
from contextlib import ExitStack

F32 = mybir.dt.float32
I32 = mybir.dt.int32
U32 = mybir.dt.uint32
ALU = mybir.AluOpType
ACT = mybir.ActivationFunctionType
AX = mybir.AxisListType

P = 128
D = 1024
KT = D // P
SEQ = 256
NS, LS = 8, 8
T = SEQ + NS * LS
TT = 3
ROWS = [P, P, T - 2 * P]
CH = 512
CT = CH // P
CA, CB = 3, 31
HEADS, HD = 4, 128
MEM = 256
NE, TOPK = 32, 4
EPS = 1e-5
LIMIT, ALPHA = 7.0, 1.702
SLOTS = 6
WIN, BLK = 128, 64
WINDOWS = -(-T // WIN)
PADA, PADB = CA - 1, CB - 1
EXTA = PADA + SEQ + NS * (PADA + LS)
EXTB = PADB + SEQ + NS * (PADB + LS)

CHUNKS = ["val", "gate", "c", "h", "k", "v", "q", "b",
          "gA0", "oA", "s0", "gA1", "s1",
          "gB0", "oB", "s2", "gB1", "s3",
          "gX0", "oX", "gX1", "wo0", "wo1"]
NMIX = len(CHUNKS)
ZCOL = {"b": 0, "c": 512, "h": 1024, "val": 1536, "gate": 2048, "q": 2560,
        "gA0": 3072, "gA1": 3584, "gB0": 4096, "gB1": 4608, "gX0": 5120, "gX1": 5632}
CPE = 6


def slot_of(n):
    return n % SLOTS


def arrived(n):
    return 16 * (n // SLOTS + 1)


def build(nc, a, o):
    with ExitStack() as ctx:
        program(nc, a, o, ctx)


def program(nc, a, o, ctx):
    def sb(name, shape, dt=F32):
        return ctx.enter_context(nc.sbuf_tensor(name, shape, dt))

    def sem(name):
        return ctx.enter_context(nc.semaphore(name))

    ring = sb("ring", [P, SLOTS, 4096])
    X = sb("X", [P, TT, D])
    XN = sb("XN", [P, TT, D])
    arena = sb("arena", [P, 19872])
    PS = ctx.enter_context(nc.psum_tensor("PS", [P, 8, 512], F32))

    def view(at, *dims):
        n = 1
        for d in dims:
            n *= d
        v = arena[:, at:at + n]
        names = "abcdef"[:len(dims)]
        if len(dims) > 1:
            v = v.rearrange(f"p ({' '.join(names)}) -> p {' '.join(names)}",
                            **{names[i]: dims[i] for i in range(1, len(dims))})
        return v

    hT = view(0, KT, T)
    extB = view(2560, CT, EXTB)
    convB = view(4920, CT, T)
    extA = view(6200, CT, EXTA)
    convA = view(7552, CT, T)
    QW = T + 24
    qT = view(8832, HEADS, QW)
    stA = view(8832, CH)
    rowsW = view(8832 + 512, CH)
    merged = view(10208, KT, T)
    memx = view(10208, 2, D)
    sq = view(10208, CT, T)
    rs = view(10208 + CT * T, T)
    memT = view(12768, KT, MEM)
    probs = view(12768, KT, MEM)
    kvn = view(14816, 2, 2, 512)
    kT = view(16864, HEADS, MEM)
    junk = view(16864, D)
    pT = view(17888, 2, 2, MEM)
    stB = view(17888, 2, CH)
    newB = view(17888, CT, NS * PADB)
    newA = view(17888 + CT * NS * PADB, CT, NS * PADA)
    tmp = view(18912, 2, T)
    tmp2 = view(19552, T)
    xnf = XN[:, :, :].rearrange("p a b -> p (a b)")
    oT = xnf[:, 0:HEADS * T].rearrange("p (h t) -> p h t", h=HEADS)
    kTs = xnf[:, HEADS * T:HEADS * T + D].rearrange("p (h m) -> p h m", h=HEADS)
    xf = X[:, :, :].rearrange("p a b -> p (a b)")
    outB = xf[:, 0:1024].rearrange("p (a c) -> p a c", a=2)
    outBp, outA, outAp = (xf[:, 1024 + 512 * i:1536 + 512 * i] for i in range(3))
    bias = view(2560, 2, D)
    gbuf = view(4608, 2, 512)
    ubuf = view(5632, 2, 512)
    sbuf = view(6656, 2, 512)
    actT = view(7680, 2, 4, P)
    Zs = view(8704, 2, 2, 512)
    P0 = view(10752, TT, WIN)
    Pg = view(11136, TT, 2, 2, BLK)
    S = view(11904, 2, 2, T)
    xT = view(13184, 2, KT, WIN)
    normfin = view(15232, D)
    L = view(16256, TT, NE)
    top = view(16352, TT, 8)
    gates = view(16376, TT, 8)
    idxf = view(16400, TT, 8)
    idxu = view(16424, TT, 8).bitcast(U32)
    M = view(16448, TT, NE + 1)
    G = view(16547, TT, NE + 1)
    posm = view(16646, TT, NE + 1)
    gtmp = view(16745, TT, NE)
    cntf = view(16841, NE + 2)
    cnti = view(16875, NE + 2).bitcast(I32)
    maxi = view(16910, 2).bitcast(I32)
    pcol = view(16912, TT)
    gcol = view(16915, TT)
    final = XN

    ident = sb("ident", [P, P])
    ones = sb("ones", [P, P])
    onesC = sb("onesC", [P, P])
    before = sb("before", [P, P])
    iotaw = sb("iotaw", [P, WIN])
    iotad = sb("iotad", [P, 2, 2, BLK])
    CW = sb("CW", [P, CT, CA + CB + 3])
    nmix = sb("nmix", [P, KT])
    nmem = sb("nmem", [P, KT])
    nffn = sb("nffn", [P, KT])
    wr = sb("wr", [P, KT, NE])
    br = sb("br", [1, NE])
    ss = sb("ss", [P, 8])
    rstd = sb("rstd", [P, 8])
    eps = sb("eps", [P, 1])
    mx = sb("mx", [P, 12, 2])
    sm = sb("sm", [P, 12, 2])
    WB, WA, BB, LG, LB = 0, CB, CB + CA, CB + CA + 1, CB + CA + 2

    def zA(ct=slice(None)):
        return extA[:, ct, PADA + SEQ:EXTA].rearrange("p c (s l) -> p c s l", s=NS) if isinstance(ct, slice) \
            else extA[:, ct, PADA + SEQ:EXTA].rearrange("p (s l) -> p s l", s=NS)

    def zB(ct=slice(None)):
        return extB[:, ct, PADB + SEQ:EXTB].rearrange("p c (s l) -> p c s l", s=NS) if isinstance(ct, slice) \
            else extB[:, ct, PADB + SEQ:EXTB].rearrange("p (s l) -> p s l", s=NS)

    loaded = [sem(f"loaded{i}") for i in range(SLOTS)]
    chunk_used = sem("chunk_used")
    x_in, mem_in, small_in, state_in, x_again = (sem(s) for s in ("x_in", "mem_in", "small_in", "state_in", "x_again"))
    keys_in = [sem(f"keys_in{i}") for i in range(4)]
    outs, consts = sem("outs"), sem("consts")
    x_normed, mem_normed = sem("x_normed"), sem("mem_normed")
    xt_done, xt_read, mt_done, mt_read = sem("xt_done"), sem("xt_read"), sem("mt_done"), sem("mt_read")
    st_in_done, st_in_read = sem("st_in_done"), sem("st_in_read")
    z_done, z_read, pool_mul = sem("z_done"), sem("z_read"), sem("pool_mul")
    kv_done, kv_read, kt_done, kt_read = sem("kv_done"), sem("kv_read"), sem("kt_done"), sem("kt_read")
    so_packed, so_done, so_read = sem("so_packed"), sem("so_done"), sem("so_read")
    dve_chain, act_chain = sem("dve_chain"), sem("act_chain")
    convb_done, conva_done = sem("convb_done"), sem("conva_done")
    mean_done, centred, squared, var_done, ln_std, ln_scaled, branchB = (
        sem(s) for s in ("mean_done", "centred", "squared", "var_done", "ln_std", "ln_scaled", "branchB"))
    sc_done, mx_ready, exp_done, p_ready = sem("sc_done"), sem("mx_ready"), sem("exp_done"), sem("p_ready")
    pt_done, pt_read, o_done, o_read = sem("pt_done"), sem("pt_read"), sem("o_done"), sem("o_read")
    kts_done, kts_read = sem("kts_done"), sem("kts_read")
    y_done, gated, merged_ready, wo_half, wo_done, x2_ready = (
        sem(s) for s in ("y_done", "gated", "merged_ready", "wo_half", "wo_done", "x2_ready"))
    ffn_sq, ffn_normed, ht_done, ht_read, logits_done = (
        sem(s) for s in ("ffn_sq", "ffn_normed", "ht_done", "ht_read", "logits_done"))
    top_ready, exp4, masks_ready, pos_done, cnt_ready = (
        sem(s) for s in ("top_ready", "exp4", "masks_ready", "pos_done", "cnt_ready"))
    bias_in = [sem(f"bias_in{i}") for i in range(2)]
    xT_ready, gu_done, g_ready, gu_read, sig_done, prod, act_ready = (
        sem(s) for s in ("xT_ready", "gu_done", "g_ready", "gu_read", "sig_done", "prod", "act_ready"))
    tr_done, actT_ready, dn_done, zs_ready, cb_done, y_acc = (
        sem(s) for s in ("tr_done", "actT_ready", "dn_done", "zs_ready", "cb_done", "y_acc"))
    g_done, pick_ready, sel_done, S_ready, zeroed, pcol_ready = (
        sem(s) for s in ("g_done", "pick_ready", "sel_done", "S_ready", "zeroed", "pcol_ready"))
    spacer = sem("spacer")
    shifted, all_back = sem("shifted"), sem("all_back")
    fin_in, fin_out = sem("fin_in"), sem("fin_out")

    w_in = a["w_in"][0].rearrange("(p k) n -> p k n", p=P)
    w_kv = a["w_mem_kv"][0].rearrange("(p k) n -> p k n", p=P)
    w_o = a["w_o"][0].rearrange("(t p) n -> p t n", p=P)
    wgu = a["w_gu"][0].rearrange("e (p k) n -> e p k n", p=P)
    wdn = a["w_dn"][0].rearrange("e (t p) n -> e p t n", p=P)
    bgu = a["b_gu"][0].rearrange("e (g n) -> e g n", g=2)
    bdn = a["b_dn"][0].rearrange("e (g n) -> e g n", g=1)
    ck = a["cache_mem_k"][0].rearrange("s (p m) h d -> p s (m h d)", p=P)
    cv = a["cache_mem_v"][0].rearrange("s (p m) h d -> p s (m h d)", p=P)
    x_p = a["x_prompt"][0].rearrange("(t p) d -> p t d", p=P)
    x_s = a["x_sample"].rearrange("s l d -> (s l) d")

    def slot(n, k):
        return ring[:, slot_of(n), :].rearrange("p (k n) -> p k n", k=k)

    def samples(n):
        v = ring[:, slot_of(n), :].rearrange("p (f s m c) -> p f s m c", f=2, s=2, m=2)
        return v[:, 0], v[:, 1]

    block = ctx.enter_context(nc.Block())

    @block.sync
    def _(sp):
        sp.dma_start(X[:, 0:2, :], x_p).then_inc(x_in, 16)
        sp.dma_start(X[0:ROWS[2], 2, :], x_s).then_inc(x_in, 16)

        def mixer_chunk(n):
            name = CHUNKS[n]
            if n >= SLOTS:
                sp.wait_ge(*used_up[CHUNKS[n - SLOTS]])
            if name in ZCOL:
                sp.dma_start(slot(n, KT), w_in[:, :, ZCOL[name]:ZCOL[name] + 512]).then_inc(loaded[slot_of(n)], 16)
            elif name in ("k", "v"):
                c = 512 * (name == "v")
                sp.dma_start(slot(n, KT), w_kv[:, :, c:c + 512]).then_inc(loaded[slot_of(n)], 16)
            elif name[0] == "o":
                w = a["w_out_" + name[1].lower()][0].rearrange("(t p) n -> p t n", p=P)
                sp.dma_start(slot(n, 4), w).then_inc(loaded[slot_of(n)], 16)
            elif name[0] == "s":
                s = 2 * int(name[1])
                flat = ring[:, slot_of(n), :].rearrange("p (f s c) -> p f s c", f=2, s=2)
                sp.dma_start(flat[:, 0], ck[:, s:s + 2, :]).then_inc(keys_in[s // 2], 16)
                sp.dma_start(flat[:, 1], cv[:, s:s + 2, :]).then_inc(loaded[slot_of(n)], 16)
            else:
                t = 4 * int(name[2])
                sp.dma_start(slot(n, 4), w_o[:, t:t + 4, :]).then_inc(loaded[slot_of(n)], 16)

        used_up = {name: (z_done, 4 * (i + 1)) for i, name in enumerate(("val", "gate", "c", "h", "q", "b"))}
        used_up |= {"k": (kv_done, 2), "v": (kv_done, 4), "s0": (o_done, HEADS + 2), "s1": (o_done, HEADS + 4),
                    "s2": (o_done, HEADS + 6), "s3": (o_done, HEADS + 8), "wo0": (wo_half, 1), "wo1": (wo_done, 3)}
        for i, b in enumerate("ABX"):
            used_up |= {f"g{b}0": (y_done, 8 * i + 4), f"g{b}1": (y_done, 8 * i + 8), f"o{b}": (y_done, 8 * i + 8)}

        for n in range(NMIX):
            mixer_chunk(n)
            if CHUNKS[n] == "gA0":
                sp.wait_ge(kv_read, 4)
                for i, name in enumerate(("new_k", "new_v")):
                    sp.dma_start(o[name][0, 0].rearrange("(t p) h d -> p t (h d)", p=P), kvn[:, :, i, :]) \
                        .then_inc(outs, 16)
                sp.wait_ge(so_read, 5)
                for i in range(2):
                    sp.dma_start(o["new_b_sample"][0, 4 * i:4 * i + 4].rearrange("s r c -> (s r) c"),
                                 outB[0:4 * PADB, i, :]).then_inc(outs, 16)
                sp.dma_start(o["new_b_prompt"][0, 0], outBp[0:PADB, :]).then_inc(outs, 16)
                sp.dma_start(o["new_a_sample"][0].rearrange("s r c -> (s r) c"), outA[0:NS * PADA, :]) \
                    .then_inc(outs, 16)
                sp.dma_start(o["new_a_prompt"][0, 0], outAp[0:PADA, :]).then_inc(outs, 16)
                sp.wait_ge(outs, 16 * 7)
                sp.dma_start(X[:, 0:2, :], x_p).then_inc(x_again, 16)
                sp.dma_start(X[0:ROWS[2], 2, :], x_s).then_inc(x_again, 16)

        def expert_chunk(e, q, c):
            s = slot_of(NMIX + c)
            if c == 0:
                sp.dma_start(bias[0:33:32, q, :], bgu[e]).then_inc(bias_in[q], 16)
                sp.dma_start(bias[64:65, q, :], bdn[e]).then_inc(bias_in[q], 16)
            if c < 4:
                sp.dma_start(slot(s, 2), wgu[e, :, 2 * c:2 * c + 2, :]).then_inc(loaded[s], 16)
            else:
                sp.dma_start(slot(s, 4), wdn[e, :, 4 * (c - 4):4 * (c - 4) + 4, :]).then_inc(loaded[s], 16)

        def expert(e, q, n):
            for c in range(CPE):
                if c == 3:
                    sp.wait_ge(gu_done, n)
                elif c == 5:
                    sp.wait_ge(dn_done, n)
                else:
                    sp.wait_ge(chunk_used, 4 * n + (0 if c == 4 else c - 3))
                expert_chunk(e, q, c)

        for c in range(CPE):
            sp.wait_ge(*used_up[CHUNKS[NMIX - SLOTS + c]])
            expert_chunk(0, 0, c)
        expert(1, 1, 1)
        with sp.Fori(1, NE // 2) as i:
            for q in range(2):
                expert(2 * i + q, q, 2 * i + q)
        sp.wait_ge(cnt_ready, 1)
        most = sp.value_load(maxi[0:1, 0:1], min_val=0, max_val=T)
        with sp.Fori(1, WINDOWS) as w:
            with sp.If(most > WIN * w):
                with sp.Fori(0, NE // 2) as i:
                    for q in range(2):
                        expert(2 * i + q, q, NE * w + 2 * i + q)
                sp.nop()
            sp.nop()
        sp.wait_ge(fin_out, 3)
        sp.dma_start(o["y_prompt"][0].rearrange("(t p) d -> p t d", p=P), final[:, 0:2, :]).then_inc(outs, 16)
        sp.dma_start(o["y_sample"].rearrange("s l d -> (s l) d"), final[0:ROWS[2], 2, :]).then_inc(outs, 16)
        sp.wait_ge(outs, 16 * 9)

    @block.gpsimd
    def _(pool):
        nc.gpsimd.memset(ident[:], 0.0)
        nc.gpsimd.memset(before[:], 1.0)
        nc.gpsimd.memset(eps[:], EPS)
        nc.gpsimd.memset(onesC[:], 1.0 / CH)
        nc.gpsimd.memset(ones[:], 1.0).then_inc(consts, 1)
        pool.wait_ge(consts, 1)
        nc.gpsimd.affine_select(out=ident[:], in_=ident[:], compare_op=ALU.not_equal, fill=1.0, base=0,
                                pattern=[[-1, P]], channel_multiplier=1).then_inc(consts, 1)
        nc.gpsimd.affine_select(out=before[:], in_=before[:], compare_op=ALU.is_gt, fill=0.0, base=0,
                                pattern=[[1, P]], channel_multiplier=-1)
        nc.gpsimd.iota(iotaw[:], [[1, WIN]], base=0, channel_multiplier=0, allow_small_or_imprecise_dtypes=True)
        nc.gpsimd.iota(iotad[:], [[BLK, 2], [0, 2], [1, BLK]], base=0, channel_multiplier=0,
                       allow_small_or_imprecise_dtypes=True)
        nc.gpsimd.memset(extA[:, :, 0:PADA], 0.0)
        nc.gpsimd.memset(extB[:, :, 0:PADB], 0.0).then_inc(consts, 1)

        def product(j, dst_p, dst_s, k):
            pool.wait_ge(z_read, j + 1)
            t = tmp[:, j % 2, :]
            nc.gpsimd.tensor_tensor(dst_p, dst_p, t[:, 0:SEQ], ALU.mult)
            nc.gpsimd.tensor_tensor(dst_s, dst_s, t[:, SEQ:T].rearrange("p (s l) -> p s l", s=NS), ALU.mult) \
                .then_inc(pool_mul, 1)

        for ct in range(CT):
            product(4 + ct, extB[:, ct, PADB:PADB + SEQ], zB(ct)[:, :, PADB:], ct)
        for ct in range(CT):
            product(12 + ct, extA[:, ct, PADA:PADA + SEQ], zA(ct)[:, :, PADA:], 4 + ct)
        pool.wait_ge(st_in_read, 4)
        pool.wait_ge(pool_mul, 8)
        nc.gpsimd.tensor_copy(newB[:].rearrange("p c (s r) -> p c s r", s=NS), zB()[:, :, :, LS:])
        nc.gpsimd.tensor_copy(newA[:].rearrange("p c (s r) -> p c s r", s=NS), zA()[:, :, :, LS:]).then_inc(so_packed, 1)
        for ct in range(CT):
            pool.wait_ge(conva_done, ct + 1)
            product(20 + ct, convA[:, ct, 0:SEQ], convA[:, ct, SEQ:T].rearrange("p (s l) -> p s l", s=NS), 8 + ct)

        pool.wait_ge(x2_ready, 3)
        nc.gpsimd.memset(Zs[:, 1], 0.0).then_inc(zs_ready, 1)
        nc.gpsimd.memset(L[:], 0.0).then_inc(consts, 1)

        def build_selection():
            for tt in range(TT):
                nc.gpsimd.tensor_scalar(P0[:, tt, :], iotaw[:], pcol[:, tt:tt + 1], None, ALU.is_equal)
            for tt in range(TT):
                last = nc.gpsimd.tensor_scalar(Pg[:, tt], iotad[:], pcol[:, tt:tt + 1], gcol[:, tt:tt + 1],
                                               ALU.is_equal, ALU.mult)
            last.then_inc(pick_ready, 1)

        def window(w, first):
            if not first:
                pool.wait_ge(cb_done, 99 * w)
                pool.wait_ge(sel_done, 33 * w)
                pool.sem_inc(spacer, 1)
            nc.gpsimd.memset(S[:, 1], 0.0).then_inc(zeroed, 1)
            pool.wait_ge(pcol_ready, 33 * w + 1)
            pool.sem_inc(spacer, 1)
            build_selection()
            with pool.Fori(0, NE) as e:
                pool.wait_ge(sel_done, 33 * w + e + 1)
                pool.wait_ge(pcol_ready, 33 * w + e + 2)
                pool.sem_inc(spacer, 1)
                build_selection()

        window(0, True)
        pool.wait_ge(cnt_ready, 1)
        most = pool.value_load(maxi[0:1, 0:1], min_val=0, max_val=T)
        with pool.Fori(1, WINDOWS) as w:
            with pool.If(most > WIN * w):
                window(w, False)
            pool.nop()

    @block.scalar
    def _(act):
        act.dma_start(memx[:], a["mem_prompt"][0].rearrange("(t p) d -> p t d", p=P)).then_inc(mem_in, 16)
        act.dma_start(nmix[:], a["norm_mix"][0].rearrange("(p k) -> p k", p=P)).then_inc(small_in, 16)
        act.dma_start(nmem[:], a["norm_mem"][0].rearrange("(p k) -> p k", p=P)).then_inc(small_in, 16)
        act.dma_start(nffn[:], a["norm_ffn"][0].rearrange("(p k) -> p k", p=P)).then_inc(small_in, 16)
        act.dma_start(rowsW[0:CB, :], a["w_conv_b"][0]).then_inc(small_in, 16)
        act.dma_start(rowsW[WA:WA + CA, :], a["w_conv_a"][0]).then_inc(small_in, 16)
        act.dma_start(rowsW[BB:BB + 1, :], a["b_conv_b"]).then_inc(small_in, 16)
        act.dma_start(rowsW[LG:LG + 1, :], a["ln_conv_b_g"]).then_inc(small_in, 16)
        act.dma_start(rowsW[LB:LB + 1, :], a["ln_conv_b_b"]).then_inc(small_in, 16)
        act.dma_start(wr[:], a["w_router"][0].rearrange("(p k) e -> p k e", p=P)).then_inc(small_in, 16)
        act.dma_start(br[:], a["b_router"]).then_inc(small_in, 16)
        act.dma_start(stA[0:NS * PADA, :], a["state_conv_a"][0].rearrange("s r c -> (s r) c")).then_inc(state_in, 16)
        for i in range(2):
            act.dma_start(stB[0:4 * PADB, i, :],
                          a["state_conv_b"][0, 4 * i:4 * i + 4].rearrange("s r c -> (s r) c")).then_inc(state_in, 16)

        chain = [0]

        def link(ins):
            chain[0] += 1
            ins.then_inc(act_chain, 1)
            act.wait_ge(act_chain, chain[0])

        act.wait_ge(x_in, 32)
        act.wait_ge(consts, 1)
        for tt in range(TT):
            link(nc.scalar.activation(junk[0:ROWS[tt], :], X[0:ROWS[tt], tt, :], ACT.Square,
                                      accum_out=ss[0:ROWS[tt], tt:tt + 1]))
        act.wait_ge(mem_in, 16)
        for mt in range(2):
            link(nc.scalar.activation(junk[:], memx[:, mt, :], ACT.Square, accum_out=ss[:, 3 + mt:4 + mt]))
        for c0, c1, rows in ((0, 2, P), (2, 3, ROWS[2]), (3, 5, P)):
            nc.scalar.activation(ss[0:rows, c0:c1], ss[0:rows, c0:c1], ACT.Sqrt, bias=eps[0:rows, :],
                                 scale=1.0 / D).then_inc(ffn_sq, 1)

        act.wait_ge(small_in, 16 * 10)
        for k in range(KT):
            act.wait_ge(mt_done, k + 1)
            nc.scalar.activation(memT[:, k, :], PS[:, 4 + k % 4, 0:MEM], ACT.Copy, scale=nmem[:, k:k + 1]) \
                .then_inc(mt_read, 1)

        zj = [0]

        def z_tile():
            j = zj[0]
            zj[0] += 1
            act.wait_ge(z_done, j + 1)
            return j, PS[:, j % 2, 0:T]

        def split(dst_p, dst_s, z):
            nc.scalar.activation(dst_p, z[:, 0:SEQ], ACT.Copy)
            return nc.scalar.activation(dst_s, z[:, SEQ:T].rearrange("p (s l) -> p s l", s=NS), ACT.Copy)

        def to_tmp(func, free_at=None):
            j, z = z_tile()
            if free_at is not None:
                act.wait_ge(*free_at)
            nc.scalar.activation(tmp[:, j % 2, :], z, func).then_inc(z_read, 1)

        for ct in range(CT):
            j, z = z_tile()
            split(extB[:, ct, PADB:PADB + SEQ], zB(ct)[:, :, PADB:], z).then_inc(z_read, 1)
        for ct in range(CT):
            to_tmp(ACT.Sigmoid, (pool_mul, ct - 1) if ct >= 2 else None)
        for ct in range(CT):
            j, z = z_tile()
            split(extA[:, ct, PADA:PADA + SEQ], zA(ct)[:, :, PADA:], z).then_inc(z_read, 1)
        for ct in range(CT):
            to_tmp(ACT.Copy, (pool_mul, 4 + ct - 1))
        for i in range(4):
            act.wait_ge(kv_done, i + 1)
            nc.scalar.activation(kvn[:, i % 2, i // 2, :], PS[:, 4 + i, :], ACT.Copy).then_inc(kv_read, 1)
        for i in range(2):
            act.wait_ge(kt_done, i + 1)
            nc.scalar.activation(kT[:, 2 * i:2 * i + 2, :].rearrange("p h m -> p (h m)"), PS[:, 4 + i, :], ACT.Copy) \
                .then_inc(kt_read, 1)
        act.wait_ge(xt_read, 8)
        for i, (dst, n) in enumerate(((outB[:, 0], 4 * PADB), (outB[:, 1], 4 * PADB), (outBp, PADB),
                                      (outA, NS * PADA), (outAp, PADA))):
            act.wait_ge(so_done, i + 1)
            nc.scalar.activation(dst[0:n, :], PS[0:n, 6 + i % 2, :], ACT.Copy).then_inc(so_read, 1)
        for h in range(HEADS):
            j, z = z_tile()
            nc.scalar.activation(qT[:, h, 0:T], z, ACT.Copy).then_inc(z_read, 1)
        for ct in range(CT):
            to_tmp(ACT.Copy, (pool_mul, 8 + max(ct - 1, 0)))

        act.wait_ge(centred, 1)
        nc.scalar.activation(sq[:], convB[:], ACT.Square).then_inc(squared, 1)
        SC = float(HD) ** -0.5

        def exps(i, units, psum, dst):
            for u in range(units):
                last = nc.scalar.activation(dst[:, u, :], psum[:, u * MEM:(u + 1) * MEM], ACT.Exp,
                                            bias=mx[:, i, u:u + 1], scale=SC, accum_out=sm[:, i, u:u + 1])
            last.then_inc(exp_done, 1)

        for h in range(HEADS):
            act.wait_ge(mx_ready, h + 1)
            exps(h, 2, PS[:, 4 + h, :], probs[:, 2 * h:2 * h + 2, :])
        act.wait_ge(var_done, 1)
        nc.scalar.activation(rs[:], PS[:, 3, 0:T], ACT.Sqrt, bias=eps[:]).then_inc(ln_std, 1)
        for h in range(HEADS):
            act.wait_ge(pt_done, h + 1)
            if h >= 2:
                act.wait_ge(o_done, h - 1)
            nc.scalar.activation(pT[:, h % 2].rearrange("p m t -> p (m t)"), PS[:, 4 + h, :], ACT.Copy) \
                .then_inc(pt_read, 1)
        act.wait_ge(ln_scaled, 1)
        for ct in range(CT):
            nc.scalar.activation(convB[:, ct, :], convB[:, ct, :], ACT.Silu, bias=CW[:, ct, LB:LB + 1],
                                 scale=CW[:, ct, LG:LG + 1]).then_inc(branchB, 1)

        def gate_tile(g):
            if g == 0:
                act.wait_ge(pool_mul, 12)
            to_tmp(ACT.Sigmoid, (gated, g - 1) if g >= 2 else None)

        def keys_t(s):
            act.wait_ge(kts_done, s + 1)
            act.wait_ge(sc_done, HEADS + s)
            nc.scalar.activation(kTs[:].rearrange("p h m -> p (h m)"), PS[:, 4:6, :].rearrange("p a b -> p (a b)"),
                                 ACT.Copy).then_inc(kts_read, 1)

        def sample_exp(s):
            i = HEADS + s
            act.wait_ge(mx_ready, i + 1)
            act.wait_ge(pt_done, i - 1)
            exps(i, 1, PS[:, 6, :], probs[:, s % 2:s % 2 + 1, :])

        def sample_pt(s):
            i = HEADS + s
            act.wait_ge(pt_done, i + 1)
            act.wait_ge(o_done, i - 1)
            nc.scalar.activation(pT[:, s % 2].rearrange("p m t -> p (m t)")[:, 0:MEM], PS[:, 7, 0:MEM], ACT.Copy) \
                .then_inc(pt_read, 1)

        for g in range(16):
            gate_tile(g)
            s = g // 2
            if g % 2 == 0:
                keys_t(s)
                if s >= 1:
                    sample_pt(s - 1)
            else:
                sample_exp(s)
        sample_pt(NS - 1)
        for g in range(16, 24):
            gate_tile(g)

        for tt in range(TT):
            act.wait_ge(x2_ready, tt + 1)
            link(nc.scalar.activation(junk[0:ROWS[tt], :], X[0:ROWS[tt], tt, :], ACT.Square,
                                      accum_out=ss[0:ROWS[tt], tt:tt + 1]))
        for c0, c1, rows in ((0, 2, P), (2, 3, ROWS[2])):
            nc.scalar.activation(ss[0:rows, c0:c1], ss[0:rows, c0:c1], ACT.Sqrt, bias=eps[0:rows, :],
                                 scale=1.0 / D).then_inc(ffn_sq, 1)
        act.dma_start(normfin[:], a["norm_final"].partition_broadcast(P)).then_inc(fin_in, 16)
        for k in range(1, KT, 2):
            act.wait_ge(ht_done, k + 1)
            nc.scalar.activation(hT[:, k, :], PS[:, k, 0:T], ACT.Copy, scale=nffn[:, k:k + 1]).then_inc(ht_read, 1)
        act.wait_ge(top_ready, 1)
        for tt in range(TT):
            last = nc.scalar.activation(gates[:, tt, 0:TOPK], top[:, tt, 0:TOPK], ACT.Exp,
                                        bias=ss[:, 4 + tt:5 + tt], accum_out=rstd[:, 4 + tt:5 + tt])
        last.then_inc(exp4, 1)

        def move_tokens(w, e, q):
            act.wait_ge(g_done, 33 * w + e + 1)
            for k in range(KT):
                last = nc.scalar.activation(xT[:, q, k, :], PS[:, 6 + k // 4, (k % 4) * WIN:(k % 4 + 1) * WIN],
                                            ACT.Copy, scale=nffn[:, k:k + 1])
            last.then_inc(xT_ready, 1)

        def move_selection(w, e, q):
            act.wait_ge(sel_done, 33 * w + e + 1)
            nc.scalar.activation(S[:, q], PS[:, 6:8, 0:T], ACT.Copy).then_inc(S_ready, 1)

        def window(w):
            move_tokens(w, 0, 0)
            move_selection(w, 0, 0)
            with act.Fori(0, NE // 2) as i:
                for q in range(2):
                    e = 2 * i + q
                    act.wait_ge(g_ready, NE * w + e + 1)
                    nc.scalar.activation(sbuf[:], gbuf[:], ACT.Sigmoid, scale=ALPHA).then_inc(sig_done, 1)
                    move_tokens(w, e + 1, 1 - q)
                    act.wait_ge(tr_done, NE * w + e + 1)
                    nc.scalar.activation(actT[:].rearrange("p b j t -> p b (j t)"), PS[:, 4:6, :], ACT.Copy) \
                        .then_inc(actT_ready, 1)
                    act.wait_ge(dn_done, NE * w + e + 1)
                    nc.scalar.activation(Zs[:, q], PS[:, 4:6, :], ACT.Copy).then_inc(zs_ready, 1)
                    move_selection(w, e + 1, 1 - q)

        window(0)
        act.wait_ge(cnt_ready, 1)
        most = act.value_load(maxi[0:1, 0:1], min_val=0, max_val=T)
        with act.Fori(1, WINDOWS) as w:
            with act.If(most > WIN * w):
                window(w)
            act.nop()

        act.wait_ge(all_back, 1)
        for tt in range(TT):
            link(nc.scalar.activation(gbuf[0:ROWS[tt]].rearrange("p a b -> p (a b)"), X[0:ROWS[tt], tt, :],
                                      ACT.Square, accum_out=ss[0:ROWS[tt], tt:tt + 1]))
        for c0, c1, rows in ((0, 2, P), (2, 3, ROWS[2])):
            nc.scalar.activation(ss[0:rows, c0:c1], ss[0:rows, c0:c1], ACT.Sqrt, bias=eps[0:rows, :],
                                 scale=1.0 / D).then_inc(ffn_sq, 1)

    @block.vector
    def _(dve):
        chain = [0]

        def tick(ins):
            chain[0] += 1
            ins.then_inc(dve_chain, 1)
            return chain[0]

        def link(ins):
            dve.wait_ge(dve_chain, tick(ins))

        dve.wait_ge(ffn_sq, 3)
        for c0, c1, rows in ((0, 2, P), (2, 3, ROWS[2]), (3, 5, P)):
            link(nc.vector.reciprocal(rstd[0:rows, c0:c1], ss[0:rows, c0:c1]))
        for tt in range(TT):
            nc.vector.tensor_scalar(XN[0:ROWS[tt], tt, :], X[0:ROWS[tt], tt, :], rstd[0:ROWS[tt], tt:tt + 1], None,
                                    ALU.mult).then_inc(x_normed, 1)
        for mt in range(2):
            nc.vector.tensor_scalar(memx[:, mt, :], memx[:, mt, :], rstd[:, 3 + mt:4 + mt], None, ALU.mult) \
                .then_inc(mem_normed, 1)
        dve.wait_ge(small_in, 16 * 10)
        for k in range(KT):
            dve.wait_ge(xt_done, k + 1)
            nc.vector.tensor_scalar(hT[:, k, :], PS[:, k % 4, 0:T], nmix[:, k:k + 1], None, ALU.mult) \
                .then_inc(xt_read, 1)
        dve.wait_ge(st_in_done, 1)
        nc.vector.tensor_copy(CW[:], PS[:, 7, 0:CT * (LB + 1)].rearrange("p (c r) -> p c r", c=CT)) \
            .then_inc(st_in_read, 1)
        dve.wait_ge(st_in_done, 2)
        nc.vector.tensor_copy(zA()[:, :, :, 0:PADA],
                              PS[:, 4, 0:CT * NS * PADA].rearrange("p (c s r) -> p c s r", c=CT, s=NS)) \
            .then_inc(st_in_read, 1)
        for i in range(2):
            dve.wait_ge(st_in_done, 3 + i)
            nc.vector.tensor_copy(zB()[:, :, 4 * i:4 * i + 4, 0:PADB],
                                  PS[:, 5 + i, 0:CT * 4 * PADB].rearrange("p (c s r) -> p c s r", c=CT, s=4)) \
                .then_inc(st_in_read, 1)
        link(nc.vector.memset(qT[:, :, T:QW], 0.0))
        dve.wait_ge(consts, 3)
        dve.wait_ge(st_in_read, 4)

        def conv(width, ext, zs, out, w0, pad, ct, bias_col, done):
            prev = None
            out_s = out[:, ct, SEQ:T].rearrange("p (s l) -> p s l", s=NS)
            for t in range(width):
                wt = CW[:, ct, w0 + t:w0 + t + 1]
                for dst, src in ((out[:, ct, 0:SEQ], ext[:, ct, t:t + SEQ]), (out_s, zs[:, :, t:t + LS])):
                    if t >= 1:
                        dve.wait_ge(dve_chain, chain[0] - 1)
                    if t == 0:
                        if bias_col is None:
                            ins = nc.vector.tensor_scalar(dst, src, wt, None, ALU.mult)
                        else:
                            ins = nc.vector.tensor_scalar(dst, src, wt, bias_col, ALU.mult, ALU.add)
                    else:
                        ins = nc.vector.scalar_tensor_tensor(dst, src, wt, dst, ALU.mult, ALU.add)
                    tick(ins)
            dve.wait_ge(dve_chain, chain[0])
            dve.sem_inc(done, 1)

        for ct in range(CT):
            dve.wait_ge(pool_mul, ct + 1)
            conv(CB, extB, zB(ct), convB, WB, PADB, ct, CW[:, ct, BB:BB + 1], convb_done)
        for ct in range(CT):
            dve.wait_ge(pool_mul, 4 + ct + 1)
            conv(CA, extA, zA(ct), convA, WA, PADA, ct, None, conva_done)

        dve.wait_ge(mean_done, 1)
        for ct in range(CT):
            last = nc.vector.tensor_tensor(convB[:, ct, :], convB[:, ct, :], PS[:, 2, 0:T], ALU.subtract)
        last.then_inc(centred, 1)

        SC = float(HD) ** -0.5

        def maxima(i, units, psum):
            dve.wait_ge(sc_done, i + 1)
            link(nc.vector.tensor_reduce(mx[:, i, 0:units], psum, AX.X, ALU.max))
            nc.vector.tensor_scalar(mx[:, i, 0:units], mx[:, i, 0:units], -SC, None, ALU.mult).then_inc(mx_ready, 1)

        def normalise(i, units, dst):
            dve.wait_ge(exp_done, i + 1)
            link(nc.vector.reciprocal(sm[:, i, 0:units], sm[:, i, 0:units]))
            for u in range(units):
                last = nc.vector.tensor_scalar(dst[:, u, :], dst[:, u, :], sm[:, i, u:u + 1], None, ALU.mult)
            last.then_inc(p_ready, 1)

        for h in range(HEADS):
            maxima(h, 2, PS[:, 4 + h, :].rearrange("p (u m) -> p u m", u=2))
            if h >= 1:
                normalise(h - 1, 2, probs[:, 2 * h - 2:2 * h, :])
        normalise(HEADS - 1, 2, probs[:, 2 * HEADS - 2:2 * HEADS, :])
        dve.wait_ge(ln_std, 1)
        link(nc.vector.reciprocal(rs[:], rs[:]))
        for ct in range(CT):
            last = nc.vector.tensor_tensor(convB[:, ct, :], convB[:, ct, :], rs[:], ALU.mult)
        last.then_inc(ln_scaled, 1)
        for h in range(HEADS):
            dve.wait_ge(o_done, h + 1)
            nc.vector.tensor_copy(oT[:, h, 0:SEQ], PS[:, 4 + h, 0:SEQ]).then_inc(o_read, 1)

        def gate_tile(g):
            b, m = g // 8, g % 8
            dve.wait_ge(y_done, g + 1)
            dve.wait_ge(z_read, 24 + g + 1)
            if b == 0:
                nc.vector.tensor_tensor(merged[:, m, :], PS[:, 2 + g % 2, 0:T], tmp[:, g % 2, :], ALU.mult) \
                    .then_inc(gated, 1)
            else:
                if g > 8:
                    dve.wait_ge(merged_ready, g - 8)
                nc.vector.tensor_tensor(tmp2[:], PS[:, 2 + g % 2, 0:T], tmp[:, g % 2, :], ALU.mult).then_inc(gated, 1)
                dve.wait_ge(gated, g + 1)
                nc.vector.tensor_tensor(merged[:, m, :], merged[:, m, :], tmp2[:], ALU.add).then_inc(merged_ready, 1)

        def sample_out(s):
            dve.wait_ge(o_done, HEADS + s + 1)
            nc.vector.tensor_copy(oT[:, :, SEQ + LS * s:SEQ + LS * (s + 1)],
                                  PS[:, 7, 0:HEADS * LS].rearrange("p (h l) -> p h l", h=HEADS)).then_inc(o_read, 1)

        for g in range(16):
            gate_tile(g)
            s = g // 2
            if g % 2 == 1:
                maxima(HEADS + s, 1, PS[:, 6, 0:MEM].rearrange("p (u m) -> p u m", u=1))
                normalise(HEADS + s, 1, probs[:, s % 2:s % 2 + 1, :])
                if s >= 1:
                    sample_out(s - 1)
        sample_out(NS - 1)
        for g in range(16, 24):
            gate_tile(g)
        dve.wait_ge(x_again, 32)
        for tt in range(TT):
            r = ROWS[tt]
            dve.wait_ge(wo_done, tt + 1)
            nc.vector.tensor_tensor(X[0:r, tt, :].rearrange("p (a b) -> p a b", a=2), PS[0:r, 2 * tt:2 * tt + 2, :],
                                    X[0:r, tt, :].rearrange("p (a b) -> p a b", a=2), ALU.add).then_inc(x2_ready, 1)
        dve.wait_ge(ffn_sq, 5)
        for c0, c1, rows in ((0, 2, P), (2, 3, ROWS[2])):
            link(nc.vector.reciprocal(rstd[0:rows, c0:c1], ss[0:rows, c0:c1]))
        for tt in range(TT):
            nc.vector.tensor_scalar(XN[0:ROWS[tt], tt, :], X[0:ROWS[tt], tt, :], rstd[0:ROWS[tt], tt:tt + 1], None,
                                    ALU.mult).then_inc(ffn_normed, 1)
        for k in range(0, KT, 2):
            dve.wait_ge(ht_done, k + 1)
            nc.vector.tensor_scalar(hT[:, k, :], PS[:, k, 0:T], nffn[:, k:k + 1], None, ALU.mult).then_inc(ht_read, 1)

        dve.wait_ge(logits_done, 1)
        dve.wait_ge(consts, 4)
        nc.vector.tensor_copy(L[:, 0:2, :], PS[:, 0, 0:2 * NE].rearrange("p (t e) -> p t e", t=2))
        link(nc.vector.tensor_copy(L[0:ROWS[2], 2, :], PS[0:ROWS[2], 0, 2 * NE:3 * NE]))
        for tt in range(TT):
            last = nc.vector.max(top[:, tt, :], L[:, tt, :])
        link(last)
        for tt in range(TT):
            nc.vector.max_index(idxu[:, tt, :], top[:, tt, :], L[:, tt, :])
        last = nc.vector.tensor_scalar(ss[:, 4:4 + TT], top[:, :, 0], -1.0, None, ALU.mult)
        last.then_inc(top_ready, 1)
        dve.wait_ge(top_ready, 1)
        link(nc.vector.tensor_copy(idxf[:], idxu[:]))
        iota_e = iotaw[:, 0:NE]
        nc.vector.memset(M[:, :, NE:NE + 1], 0.0)
        nc.vector.memset(G[:, :, NE:NE + 1], 0.0)
        for j in range(TOPK):
            for tt in range(TT):
                i1 = idxf[:, tt, j:j + 1]
                if j == 0:
                    last = nc.vector.tensor_scalar(M[:, tt, 0:NE], iota_e, i1, None, ALU.is_equal)
                else:
                    last = nc.vector.scalar_tensor_tensor(M[:, tt, 0:NE], iota_e, i1, M[:, tt, 0:NE], ALU.is_equal,
                                                          ALU.add)
            link(last)
        nc.vector.memset(gtmp[:, 0, 0:1], 0.0).then_inc(masks_ready, 1)
        dve.wait_ge(exp4, 1)
        link(nc.vector.reciprocal(rstd[:, 4:4 + TT], rstd[:, 4:4 + TT]))
        for tt in range(TT):
            last = nc.vector.tensor_scalar(gates[:, tt, 0:TOPK], gates[:, tt, 0:TOPK], rstd[:, 4 + tt:5 + tt], None,
                                           ALU.mult)
        link(last)
        for j in range(TOPK):
            for tt in range(TT):
                dst = G[:, tt, 0:NE] if j == 0 else gtmp[:, tt, :]
                last = nc.vector.tensor_scalar(dst, iota_e, idxf[:, tt, j:j + 1], gates[:, tt, j:j + 1],
                                               ALU.is_equal, ALU.mult)
            link(last)
            if j:
                link(nc.vector.tensor_tensor(G[:, :, 0:NE], G[:, :, 0:NE], gtmp[:], ALU.add))
        dve.wait_ge(pos_done, 1)
        nc.vector.memset(posm[:, :, NE:NE + 1], -1.0)
        for tt in range(TT):
            r = ROWS[tt]
            last = nc.vector.scalar_tensor_tensor(posm[0:r, tt, 0:NE], PS[0:r, 1, tt * NE:(tt + 1) * NE], 1.0,
                                                  M[0:r, tt, 0:NE], ALU.add, ALU.mult)
        link(last)
        for tt in range(TT):
            r = ROWS[tt]
            last = nc.vector.tensor_scalar(posm[0:r, tt, 0:NE], posm[0:r, tt, 0:NE], -1.0, None, ALU.add)
        link(last)
        link(nc.vector.memset(posm[ROWS[2]:P, 2, :], -1.0))
        nc.vector.memset(cntf[:, 0:1], 0.0)
        link(nc.vector.tensor_copy(cntf[:, 1:NE + 1], PS[:, 1, TT * NE:(TT + 1) * NE]))
        link(nc.vector.tensor_reduce(cntf[:, NE + 1:NE + 2], cntf[:, 1:NE + 1], AX.X, ALU.max))
        nc.vector.tensor_copy(cnti[:], cntf[:])
        nc.vector.tensor_copy(maxi[:, 0:1], cntf[:, NE + 1:NE + 2]).then_inc(cnt_ready, 1)
        nc.vector.memset(gtmp[:, 0, 0:1], 0.0).then_inc(y_acc, 3)

        def columns(e):
            nc.vector.tensor_copy(pcol[:], posm[:, :, bass.ds(e, 1)].rearrange("p t o -> p (t o)"))
            nc.vector.tensor_copy(gcol[:], G[:, :, bass.ds(e, 1)].rearrange("p t o -> p (t o)")) \
                .then_inc(pcol_ready, 1)

        def put_back(w, c):
            for tt in range(TT):
                r = ROWS[tt]
                b = (0, 2, 6)[tt]
                dve.wait_ge(cb_done, 99 * w + 3 * c + (tt + 1))
                dve.wait_ge(y_acc, 99 * w + 3 * c + (tt + 1))
                x = X[0:r, tt, :].rearrange("p (a b) -> p a b", a=2)
                nc.vector.tensor_tensor(x, PS[0:r, b:b + 2, :], x, ALU.add).then_inc(y_acc, 1)

        def window(w, first):
            if not first:
                dve.wait_ge(pick_ready, 33 * w)
                dve.wait_ge(cb_done, 99 * w)
                nc.vector.tensor_scalar(posm[:], posm[:], float(-WIN), None, ALU.add).then_inc(shifted, 1)
                nc.vector.tensor_scalar(cntf[:], cntf[:], float(-WIN), 0.0, ALU.add, ALU.max).then_inc(shifted, 1)
                dve.wait_ge(shifted, 2 * w)
                nc.vector.tensor_copy(cnti[:], cntf[:]).then_inc(cnt_ready, 1)
            columns(0)
            with dve.Fori(0, NE // 2) as i:
                for q in range(2):
                    e = 2 * i + q
                    n = NE * w + e
                    dve.wait_ge(pick_ready, 33 * w + e + 1)
                    columns(e + 1)
                    dve.wait_ge(gu_done, n + 1)
                    nc.vector.tensor_scalar(gbuf[:], PS[:, 0:2, :], LIMIT, None, ALU.min).then_inc(g_ready, 1)
                    nc.vector.tensor_scalar(ubuf[:], PS[:, 2:4, :], LIMIT, -LIMIT, ALU.min, ALU.max) \
                        .then_inc(gu_read, 1)
                    dve.wait_ge(gu_read, n + 1)
                    nc.vector.scalar_tensor_tensor(ubuf[:], ubuf[:], 1.0, gbuf[:], ALU.add, ALU.mult) \
                        .then_inc(prod, 1)
                    dve.wait_ge(prod, n + 1)
                    dve.wait_ge(sig_done, n + 1)
                    nc.vector.tensor_tensor(ubuf[:], ubuf[:], sbuf[:], ALU.mult).then_inc(act_ready, 1)
                    put_back(w, e)
            put_back(w, NE)
            dve.wait_ge(y_acc, 99 * w + 102)
            dve.sem_inc(spacer, 1)

        window(0, True)
        most = dve.value_load(maxi[0:1, 0:1], min_val=0, max_val=T)
        with dve.Fori(1, WINDOWS) as w:
            with dve.If(most > WIN * w):
                window(w, False)
            dve.nop()
        nc.vector.memset(gtmp[:, 0, 0:1], 0.0).then_inc(all_back, 1)
        dve.wait_ge(ffn_sq, 7)
        for c0, c1, rows in ((0, 2, P), (2, 3, ROWS[2])):
            link(nc.vector.reciprocal(rstd[0:rows, c0:c1], ss[0:rows, c0:c1]))
        dve.wait_ge(fin_in, 16)
        for tt in range(TT):
            r = ROWS[tt]
            nc.vector.scalar_tensor_tensor(final[0:r, tt, :], X[0:r, tt, :], rstd[0:r, tt:tt + 1], normfin[0:r, :],
                                           ALU.mult, ALU.mult).then_inc(fin_out, 1)

    @block.tensor
    def _(pe):
        mm = nc.tensor.matmul

        def tr(out, in_):
            n = in_.shape[0]
            return nc.tensor.transpose(out, in_, ident[0:n, 0:n])

        pe.wait_ge(consts, 3)
        pe.wait_ge(x_normed, 3)
        for k in range(KT):
            if k >= 4:
                pe.wait_ge(xt_read, k - 3)
            for tt in range(TT):
                r = ROWS[tt]
                last = tr(PS[:, k % 4, tt * P:tt * P + r], XN[0:r, tt, k:D:KT])
            last.then_inc(xt_done, 1)
        pe.wait_ge(mem_normed, 2)
        for k in range(KT):
            if k >= 4:
                pe.wait_ge(mt_read, k - 3)
            for mt in range(2):
                last = tr(PS[:, 4 + k % 4, mt * P:(mt + 1) * P], memx[:, mt, k:D:KT])
            last.then_inc(mt_done, 1)
        pe.wait_ge(small_in, 16 * 10)
        pe.wait_ge(state_in, 16 * 3)
        pe.wait_ge(mt_read, KT)
        for ct in range(CT):
            last = tr(PS[:, 7, ct * (LB + 1):(ct + 1) * (LB + 1)], rowsW[0:LB + 1, ct * P:(ct + 1) * P])
        last.then_inc(st_in_done, 1)
        for ct in range(CT):
            n = NS * PADA
            last = tr(PS[:, 4, ct * n:(ct + 1) * n], stA[0:n, ct * P:(ct + 1) * P])
        last.then_inc(st_in_done, 1)
        for i in range(2):
            for ct in range(CT):
                n = 4 * PADB
                last = tr(PS[:, 5 + i, ct * n:(ct + 1) * n], stB[0:n, i, ct * P:(ct + 1) * P])
            last.then_inc(st_in_done, 1)

        def arrive(n):
            pe.wait_ge(loaded[slot_of(n)], arrived(n))

        def chunk(name):
            return CHUNKS.index(name)

        zj = [0]

        def z_tile(n, m):
            j = zj[0]
            zj[0] += 1
            if j >= 2:
                pe.wait_ge(z_read, j - 1)
            w = slot(n, KT)
            for k in range(KT):
                last = mm(PS[:, j % 2, 0:T], w[:, k, m * P:(m + 1) * P], hT[:, k, :], start=k == 0, stop=k == KT - 1)
            last.then_inc(z_done, 1)
            return last

        def z_chunk(name):
            n = chunk(name)
            arrive(n)
            for m in range(4):
                z_tile(n, m)

        pe.wait_ge(xt_read, KT)
        for name in ("val", "gate", "c", "h"):
            z_chunk(name)
        pe.wait_ge(st_in_read, 4)
        for i, name in enumerate(("k", "v")):
            n = chunk(name)
            arrive(n)
            w = slot(n, KT)
            for mt in range(2):
                for k in range(KT):
                    last = mm(PS[:, 4 + 2 * i + mt, :], memT[:, k, mt * P:(mt + 1) * P], w[:, k, :],
                              start=k == 0, stop=k == KT - 1)
                last.then_inc(kv_done, 1)
        pe.wait_ge(kv_read, 2)
        for h in range(HEADS):
            for mt in range(2):
                c = (h % 2) * MEM + mt * P
                last = tr(PS[:, 4 + h // 2, c:c + P], kvn[:, mt, 0, h * P:(h + 1) * P])
            if h % 2:
                last.then_inc(kt_done, 1)
        pe.wait_ge(pool_mul, 8)
        pe.wait_ge(kv_read, 4)
        pe.wait_ge(so_packed, 1)
        sources = [lambda ct: newB[:, ct, 0:4 * PADB], lambda ct: newB[:, ct, 4 * PADB:],
                   lambda ct: extB[:, ct, SEQ:SEQ + PADB], lambda ct: newA[:, ct, :],
                   lambda ct: extA[:, ct, SEQ:SEQ + PADA]]
        for i, (src, n) in enumerate(zip(sources, (4 * PADB, 4 * PADB, PADB, NS * PADA, PADA))):
            if i >= 2:
                pe.wait_ge(so_read, i - 1)
            for ct in range(CT):
                last = tr(PS[0:n, 6 + i % 2, ct * P:(ct + 1) * P], src(ct))
            last.then_inc(so_done, 1)
        z_chunk("q")
        z_chunk("b")
        pe.wait_ge(convb_done, CT)
        for ct in range(CT):
            last = mm(PS[:, 2, 0:T], onesC[:], convB[:, ct, :], start=ct == 0, stop=ct == CT - 1)
        last.then_inc(mean_done, 1)
        pe.wait_ge(kt_read, 2)
        pe.wait_ge(so_read, 5)
        for h in range(HEADS):
            for tt in range(2):
                last = mm(PS[:, 4 + h, tt * MEM:(tt + 1) * MEM], qT[:, h, tt * P:(tt + 1) * P], kT[:, h, :],
                          start=True, stop=True)
            last.then_inc(sc_done, 1)
        pe.wait_ge(squared, 1)
        for ct in range(CT):
            last = mm(PS[:, 3, 0:T], onesC[:], sq[:, ct, :], start=ct == 0, stop=ct == CT - 1)
        last.then_inc(var_done, 1)

        def prompt_pt(h):
            pe.wait_ge(p_ready, h + 1)
            for mt in range(2):
                for tt in range(2):
                    last = tr(PS[:, 4 + h, mt * MEM + tt * P:mt * MEM + (tt + 1) * P],
                              probs[:, 2 * h + tt, mt * P:(mt + 1) * P])
            last.then_inc(pt_done, 1)

        def prompt_o(h):
            pe.wait_ge(pt_read, h + 1)
            for mt in range(2):
                last = mm(PS[:, 4 + h, 0:SEQ], kvn[:, mt, 1, h * P:(h + 1) * P], pT[:, h % 2, mt, :],
                          start=mt == 0, stop=mt == 1)
            last.then_inc(o_done, 1)

        prompt_pt(0)
        for h in range(1, HEADS):
            prompt_pt(h)
            prompt_o(h - 1)
        prompt_o(HEADS - 1)

        def sample_keys(s):
            n = chunk(f"s{s // 2}")
            arrive(n)
            pe.wait_ge(keys_in[s // 2], 16)
            if s == 0:
                pe.wait_ge(o_read, HEADS)
            else:
                pe.wait_ge(kts_read, s)
            keys = samples(n)[0][:, s % 2]
            for h in range(HEADS):
                for m in range(2):
                    c = (h % 2) * MEM + m * P
                    last = tr(PS[:, 4 + h // 2, c:c + P], keys[:, m, h * P:(h + 1) * P])
            last.then_inc(kts_done, 1)

        def sample_scores(s):
            pe.wait_ge(kts_read, s + 1)
            if s:
                pe.wait_ge(exp_done, HEADS + s)
            c = SEQ + LS * s
            for h in range(HEADS):
                last = mm(PS[32 * h:32 * h + 32, 6, 0:MEM], qT[:, h, c:c + 32], kTs[:, h, :], start=True, stop=True)
            last.then_inc(sc_done, 1)

        def sample_pt(s):
            pe.wait_ge(p_ready, HEADS + s + 1)
            pe.wait_ge(o_read, HEADS + s)
            for m in range(2):
                last = tr(PS[:, 7, m * P:(m + 1) * P], probs[:, s % 2, m * P:(m + 1) * P])
            last.then_inc(pt_done, 1)

        def sample_o(s):
            n = chunk(f"s{s // 2}")
            pe.wait_ge(pt_read, HEADS + s + 1)
            values = samples(n)[1][:, s % 2]
            pts = pT[:, s % 2].rearrange("p m t -> p (m t)")
            for h in range(HEADS):
                for m in range(2):
                    last = mm(PS[:, 7, h * LS:(h + 1) * LS], values[:, m, h * P:(h + 1) * P],
                              pts[:, m * P + 32 * h:m * P + 32 * h + LS], start=m == 0, stop=m == 1)
            last.then_inc(o_done, 1)

        ACTS = (convA, convB, oT)

        def gate_tile(g):
            b, m = g // 8, g % 8
            name = "ABX"[b]
            ng, no = chunk(f"g{name}{m // 4}"), chunk(f"o{name}")
            arrive(ng)
            z_tile(ng, m % 4)
            arrive(no)
            if g == 0:
                pe.wait_ge(pool_mul, 12)
            if g == 8:
                pe.wait_ge(branchB, CT)
            if g == 16:
                pe.wait_ge(o_read, HEADS + NS)
            if g >= 2:
                pe.wait_ge(gated, g - 1)
            w = slot(no, 4)
            for k in range(4):
                last = mm(PS[:, 2 + g % 2, 0:T], w[:, k, m * P:(m + 1) * P], ACTS[b][:, k, :], start=k == 0, stop=k == 3)
            last.then_inc(y_done, 1)

        pe.wait_ge(ln_std, 1)
        for g in range(16):
            gate_tile(g)
            s = g // 2
            if g % 2 == 0:
                sample_keys(s)
                if s >= 1:
                    sample_pt(s - 1)
            else:
                sample_scores(s)
                if s >= 1:
                    sample_o(s - 1)
        sample_pt(NS - 1)
        sample_o(NS - 1)
        for g in range(16, 24):
            gate_tile(g)

        pe.wait_ge(merged_ready, 16)
        pe.wait_ge(z_read, 48)
        for c in range(2):
            n = chunk(f"wo{c}")
            arrive(n)
            w = slot(n, 4)
            for tt in range(TT):
                r = ROWS[tt]
                for half in range(2):
                    for k in range(4):
                        last = mm(PS[0:r, 2 * tt + half, :], merged[:, 4 * c + k, tt * P:tt * P + r],
                                  w[:, k, half * 512:(half + 1) * 512], start=c == 0 and k == 0, stop=c == 1 and k == 3)
                if c == 1:
                    last.then_inc(wo_done, 1)
            if c == 0:
                last.then_inc(wo_half, 1)

        pe.wait_ge(ffn_normed, 3)
        for k in range(KT):
            for tt in range(TT):
                r = ROWS[tt]
                last = tr(PS[:, k, tt * P:tt * P + r], XN[0:r, tt, k:D:KT])
            last.then_inc(ht_done, 1)
        pe.wait_ge(ht_read, KT)
        for tt in range(TT):
            r = ROWS[tt]
            out = PS[0:r, 0, tt * NE:(tt + 1) * NE]
            for k in range(KT):
                mm(out, hT[:, k, tt * P:tt * P + r], wr[:, k, :], start=k == 0, stop=False)
            last = mm(out, ones[0:1, 0:r], br[0:1, :], start=False, stop=True)
        last.then_inc(logits_done, 1)
        pe.wait_ge(masks_ready, 1)
        for tt in range(TT):
            r = ROWS[tt]
            out = PS[0:r, 1, tt * NE:(tt + 1) * NE]
            for t0 in range(tt):
                mm(out, ones[:, 0:r], M[:, t0, 0:NE], start=t0 == 0, stop=False)
            mm(out, before[0:r, 0:r], M[0:r, tt, 0:NE], start=tt == 0, stop=True)
        for tt in range(TT):
            r = ROWS[tt]
            last = mm(PS[:, 1, TT * NE:(TT + 1) * NE], ones[0:r, :], M[0:r, tt, 0:NE], start=tt == 0, stop=tt == TT - 1)
        last.then_inc(pos_done, 1)

        def gather(w, e):
            pe.wait_ge(pick_ready, 33 * w + e + 1)
            for k in range(KT):
                out = PS[:, 6 + k // 4, (k % 4) * WIN:(k % 4 + 1) * WIN]
                for tt in range(TT):
                    r = ROWS[tt]
                    last = mm(out, XN[0:r, tt, k:D:KT], P0[0:r, tt, :], start=tt == 0, stop=tt == TT - 1)
            last.then_inc(g_done, 1)

        def turn_selection():
            for b in range(2):
                for tt in range(TT):
                    r = ROWS[tt]
                    last = tr(PS[:, 6 + b, tt * P:tt * P + r], Pg[0:r, tt, b])
            last.then_inc(sel_done, 1)

        def gate_up(n, q, blocks):
            for b in range(blocks):
                for g in range(2):
                    for h in range(2):
                        mm(PS[64 * h:64 * h + 64, 2 * g + b, :], ones[32 * g:32 * g + 1, 0:BLK],
                           bias[32 * g:32 * g + 1, q, h * 512:(h + 1) * 512], start=True, stop=False)
            for c in range(4):
                s = slot_of(NMIX + c)
                pe.wait_ge(loaded[s], 16 * n + arrived(NMIX + c))
                for kk in range(2):
                    k = 2 * c + kk
                    for b in range(blocks):
                        for g in range(2):
                            for h in range(2):
                                last = mm(PS[64 * h:64 * h + 64, 2 * g + b, :], xT[:, q, k, b * BLK:(b + 1) * BLK],
                                          slot(s, 2)[:, kk, g * D + h * 512:g * D + (h + 1) * 512],
                                          start=False, stop=k == KT - 1)
                if c < 3:
                    last.then_inc(chunk_used, 1)
            last.then_inc(gu_done, 1)

        def turn_act(blocks):
            for b in range(blocks):
                for j in range(4):
                    last = tr(PS[:, 4 + b, j * P:(j + 1) * P], ubuf[:, b, j * P:(j + 1) * P])
            last.then_inc(tr_done, 1)

        def put_back(q, blocks):
            for tt in range(TT):
                r = ROWS[tt]
                base = (0, 2, 6)[tt]
                for b in range(blocks):
                    for h in range(2):
                        last = mm(PS[0:r, base + h, :], S[64 * h:64 * h + 64, q, b, tt * P:tt * P + r],
                                  Zs[64 * h:64 * h + 64, q, b, :], start=b == 0, stop=b == blocks - 1)
                last.then_inc(cb_done, 1)

        def down(n, q, blocks):
            for b in range(blocks):
                for h in range(2):
                    mm(PS[64 * h:64 * h + 64, 4 + b, :], ones[64:65, 0:BLK], bias[64:65, q, h * 512:(h + 1) * 512],
                       start=True, stop=False)
            for c in range(2):
                s = slot_of(NMIX + 4 + c)
                pe.wait_ge(loaded[s], 16 * n + arrived(NMIX + 4 + c))
                for j in range(4):
                    for b in range(blocks):
                        for h in range(2):
                            last = mm(PS[64 * h:64 * h + 64, 4 + b, :], actT[:, b, j, c * BLK:(c + 1) * BLK],
                                      slot(s, 4)[:, j, h * 512:(h + 1) * 512], start=False, stop=c == 1 and j == 3)
                if c == 0:
                    last.then_inc(chunk_used, 1)
            last.then_inc(dn_done, 1)

        def either(count, stage, *args):
            with pe.If(count > BLK):
                stage(*args, 2)
            with pe.Else():
                stage(*args, 1)

        def window(w, first):
            pe.wait_ge(cnt_ready, w + 1)
            if first:
                pe.wait_ge(pcol_ready, 1)
            else:
                pe.wait_ge(y_acc, 99 * w + 3)
            gather(w, 0)
            pe.wait_ge(xT_ready, 33 * w + 1)
            turn_selection()
            pe.wait_ge(zeroed, w + 1)
            pe.sem_inc(spacer, 1)
            with pe.Fori(0, NE // 2) as i:
                for q in range(2):
                    e = 2 * i + q
                    n = NE * w + e
                    before_, mine = (pe.value_load(cnti[0:1, bass.ds(e + d, 1)], min_val=0, max_val=T) for d in range(2))
                    pe.wait_ge(xT_ready, 33 * w + e + 1)
                    pe.wait_ge(bias_in[q], 32 * ((NE // 2) * w + i + 1))
                    pe.wait_ge(y_acc, 99 * w + 3 * e + 2)
                    either(mine, gate_up, n, q)
                    pe.wait_ge(S_ready, 33 * w + e + 1)
                    gather(w, e + 1)
                    pe.wait_ge(act_ready, n + 1)
                    pe.wait_ge(zs_ready, n + 1)
                    either(mine, turn_act)
                    pe.wait_ge(gu_read, n + 1)
                    pe.wait_ge(xT_ready, 33 * w + e + 2)
                    either(before_, put_back, 1 - q)
                    pe.wait_ge(actT_ready, n + 1)
                    either(mine, down, n, q)
                    pe.wait_ge(y_acc, 99 * w + 3 * e + 6)
                    turn_selection()
            last_count = pe.value_load(cnti[0:1, NE:NE + 1], min_val=0, max_val=T)
            pe.wait_ge(zs_ready, NE * w + NE + 1)
            pe.wait_ge(S_ready, 33 * w + 33)
            pe.wait_ge(y_acc, 99 * w + 99)
            either(last_count, put_back, 1)

        window(0, True)
        most = pe.value_load(maxi[0:1, 0:1], min_val=0, max_val=T)
        with pe.Fori(1, WINDOWS) as w:
            with pe.If(most > WIN * w):
                window(w, False)
                pe.nop()
            pe.nop()


_INS = ["x_prompt", "x_sample", "mem_prompt", "state_conv_a", "state_conv_b", "cache_mem_k", "cache_mem_v",
        "norm_mix", "w_in", "w_conv_a", "w_out_a", "w_conv_b", "b_conv_b", "ln_conv_b_g", "ln_conv_b_b", "w_out_b",
        "norm_mem", "w_mem_kv", "w_out_x", "w_o", "norm_ffn", "w_router", "b_router", "w_gu", "b_gu", "w_dn", "b_dn",
        "norm_final"]
_OUTS = [("y_prompt", (1, SEQ, D)), ("y_sample", (NS, LS, D)), ("new_a_prompt", (1, 1, PADA, CH)),
         ("new_b_prompt", (1, 1, PADB, CH)), ("new_k", (1, 1, MEM, HEADS, HD)), ("new_v", (1, 1, MEM, HEADS, HD)),
         ("new_a_sample", (1, NS, PADA, CH)), ("new_b_sample", (1, NS, PADB, CH))]


def kernel(**inputs):
    import numpy as _np
    import concourse.bacc as _bacc
    from concourse import mybir as _mybir
    from concourse.bass_utils import run_bass_kernel_spmd as _run

    nc = _bacc.Bacc("TRN2", target_bir_lowering=False, num_devices=1)
    arrays, ins, outs = {}, {}, {}
    for name in _INS:
        x = _np.ascontiguousarray(inputs[name])
        arrays[f"in_{name}"] = x
        ins[name] = nc.dram_tensor(f"in_{name}", x.shape, _mybir.dt.from_np(x.dtype), kind="ExternalInput").ap()
    for name, shape in _OUTS:
        outs[name] = nc.dram_tensor(f"out_{name}", shape, _mybir.dt.float32, kind="ExternalOutput").ap()
    build(nc, ins, outs)
    r = _run(nc, [arrays], core_ids=[0])
    return tuple(r.results[0][f"out_{name}"] for name, _ in _OUTS)
```
